# Optimizing a Trainium2 kernel written in Bass

```python
import math
import jax
import jax.numpy as jnp
from jax import lax
import numpy as np

D_MODEL = 1024
BATCH = 1
SEQ = 2048
DEPTH = 1

D_MIX = D_MODEL
D_MLSTM = D_MIX // 2
N_MLSTM_HEADS = 4
MLSTM_HEAD_DIM = D_MLSTM // N_MLSTM_HEADS
D_CONV = D_MIX - D_MLSTM
CONV_WIDTH = 3
CHUNK = 64
FORGET_BIAS_LO = 3.0
FORGET_BIAS_HI = 6.0
N_GROUPS = 4
EXPERTS_PER_GROUP = 8
N_EXPERTS = N_GROUPS * EXPERTS_PER_GROUP
TOP_K = 2
D_FF_EXPERT = D_MODEL // 2
MOE_BLOCK = 128
RMS_EPS = 1e-6

F_OFF = 4 * D_MLSTM + N_MLSTM_HEADS
D_PROJ = 4 * D_MLSTM + 2 * N_MLSTM_HEADS + 3 * D_CONV
SPLIT_POINTS = (
    D_MLSTM,
    2 * D_MLSTM,
    3 * D_MLSTM,
    4 * D_MLSTM,
    4 * D_MLSTM + N_MLSTM_HEADS,
    4 * D_MLSTM + 2 * N_MLSTM_HEADS,
    4 * D_MLSTM + 2 * N_MLSTM_HEADS + D_CONV,
    4 * D_MLSTM + 2 * N_MLSTM_HEADS + 2 * D_CONV,
)

kernel_name = "hymba_mlstm_shortconv_hmoe_block"

def rms_norm(x, g):
    xf = x.astype(jnp.float32)
    y = xf * lax.rsqrt(jnp.mean(xf * xf, axis=-1, keepdims=True) + RMS_EPS)
    return (y * g.astype(jnp.float32)).astype(x.dtype)

def mlstm_chunkwise(q, k, v, log_i, log_f):
    b_sz, s_len, n_h, d_h = q.shape
    n_c = s_len // CHUNK

    def to_chunks(t):
        return t.reshape(b_sz, n_c, CHUNK, n_h, d_h).transpose(0, 3, 1, 2, 4)

    def gate_chunks(t):
        return t.reshape(b_sz, n_c, CHUNK, n_h).transpose(0, 3, 1, 2)

    qc, kc, vc = to_chunks(q), to_chunks(k), to_chunks(v)
    li, lf = gate_chunks(log_i), gate_chunks(log_f)

    b_cum = jnp.cumsum(lf, axis=-1)
    g_tot = b_cum[..., -1]
    a_end = g_tot[..., None] - b_cum + li
    m_loc = jnp.max(a_end, axis=-1)

    def step(carry, xs):
        c_st, n_st, m_st = carry
        k_c, v_c, a_c, g_c, ml_c = xs
        m_new = jnp.maximum(g_c + m_st, ml_c)
        decay = jnp.exp(g_c + m_st - m_new)
        w = jnp.exp(a_c - m_new[..., None])
        c_new = decay[..., None, None] * c_st + jnp.einsum('bhl,bhle,bhld->bhed', w, v_c, k_c)
        n_new = decay[..., None] * n_st + jnp.einsum('bhl,bhld->bhd', w, k_c)
        return (c_new, n_new, m_new), (c_st, n_st, m_st)

    init = (
        jnp.zeros((b_sz, n_h, d_h, d_h), jnp.float32),
        jnp.zeros((b_sz, n_h, d_h), jnp.float32),
        jnp.zeros((b_sz, n_h), jnp.float32),
    )
    xs = (
        jnp.moveaxis(kc, 2, 0),
        jnp.moveaxis(vc, 2, 0),
        jnp.moveaxis(a_end, 2, 0),
        jnp.moveaxis(g_tot, 2, 0),
        jnp.moveaxis(m_loc, 2, 0),
    )
    _, (c_prev, n_prev, m_prev) = lax.scan(step, init, xs)
    c_prev = jnp.moveaxis(c_prev, 0, 2)
    n_prev = jnp.moveaxis(n_prev, 0, 2)
    m_prev = jnp.moveaxis(m_prev, 0, -1)

    causal = jnp.tril(jnp.ones((CHUNK, CHUNK), dtype=bool))
    d_log = b_cum[..., :, None] - b_cum[..., None, :] + li[..., None, :]
    d_log = jnp.where(causal, d_log, -jnp.inf)
    inter_log = b_cum + m_prev[..., None]
    m_t = jnp.maximum(inter_log, jnp.max(d_log, axis=-1))
    scores = jnp.einsum('bhcld,bhcjd->bhclj', qc, kc) * jnp.exp(d_log - m_t[..., None])
    w_inter = jnp.exp(inter_log - m_t)
    num = jnp.einsum('bhclj,bhcje->bhcle', scores, vc) + w_inter[..., None] * jnp.einsum(
        'bhced,bhcld->bhcle', c_prev, qc)
    den = jnp.sum(scores, axis=-1) + w_inter * jnp.einsum('bhcd,bhcld->bhcl', n_prev, qc)
    h = num / jnp.maximum(jnp.abs(den), jnp.exp(-m_t))[..., None]
    return h.transpose(0, 2, 3, 1, 4).reshape(b_sz, s_len, n_h, d_h)

def short_gated_conv(gate_b, gate_c, xin, conv_w):
    u = gate_c * xin
    up = jnp.pad(u, ((0, 0), (CONV_WIDTH - 1, 0), (0, 0)))
    s_len = u.shape[1]
    z = conv_w[0] * up[:, 0:s_len] + conv_w[1] * up[:, 1:s_len + 1] + conv_w[2] * up[:, 2:s_len + 2]
    return gate_b * z

def hier_moe(h, w_group, b_group, w_expert, b_expert, w_gate, w_up, w_down):
    n_tok, d = h.shape
    hf = h.astype(jnp.float32)
    group_logits = hf @ w_group.astype(jnp.float32) + b_group.astype(jnp.float32)
    group_prob = jax.nn.softmax(group_logits, axis=-1)
    g_sel = jnp.argmax(group_logits, axis=-1)
    p_g = jnp.take_along_axis(group_prob, g_sel[:, None], axis=1)[:, 0]
    exp_logits = (hf @ w_expert.astype(jnp.float32) + b_expert.astype(jnp.float32)).reshape(
        n_tok, N_GROUPS, EXPERTS_PER_GROUP)
    in_group = jnp.take_along_axis(exp_logits, g_sel[:, None, None], axis=1)[:, 0]
    top_val, top_idx = lax.top_k(in_group, TOP_K)
    top_w = jax.nn.softmax(top_val, axis=-1) * p_g[:, None]
    expert_id = g_sel[:, None] * EXPERTS_PER_GROUP + top_idx

    nk = n_tok * TOP_K
    flat_e = expert_id.reshape(nk).astype(jnp.int32)
    flat_tok = jnp.repeat(jnp.arange(n_tok, dtype=jnp.int32), TOP_K)
    flat_w = top_w.reshape(nk).astype(h.dtype)

    counts = jnp.bincount(flat_e, length=N_EXPERTS)
    starts = jnp.cumsum(counts) - counts
    padded = ((counts + MOE_BLOCK - 1) // MOE_BLOCK) * MOE_BLOCK
    pends = jnp.cumsum(padded)
    pstarts = pends - padded
    order = jnp.argsort(flat_e)
    sorted_e = flat_e[order]
    rank = jnp.arange(nk, dtype=jnp.int32) - starts[sorted_e]
    dest = pstarts[sorted_e] + rank

    n_blocks = -(-nk // MOE_BLOCK) + N_EXPERTS
    cap = n_blocks * MOE_BLOCK
    buf_tok = jnp.zeros((cap,), jnp.int32).at[dest].set(flat_tok[order])
    buf_w = jnp.zeros((cap,), h.dtype).at[dest].set(flat_w[order])
    block_start = jnp.arange(n_blocks, dtype=jnp.int32) * MOE_BLOCK
    block_e = jnp.clip(jnp.searchsorted(pends, block_start, side='right'), 0, N_EXPERTS - 1)

    xb = h[buf_tok].reshape(n_blocks, MOE_BLOCK, d)

    def expert_block(args):
        x_blk, e = args
        a = x_blk @ w_gate[e]
        u = x_blk @ w_up[e]
        return (jax.nn.silu(a) * u) @ w_down[e]

    yb = lax.map(expert_block, (xb, block_e)).reshape(cap, d)
    return jnp.zeros((n_tok, d), h.dtype).at[buf_tok].add(buf_w[:, None] * yb)

def hybrid_layer(x, norm_mix, w_in, b_in, conv_w, w_out, norm_ffn,
                 w_group, b_group, w_expert, b_expert, w_gate, w_up, w_down):
    b_sz, s_len, d = x.shape
    hn = rms_norm(x, norm_mix)
    proj = hn @ w_in + b_in
    q, k, v, o, ig, fg, cb, cc, cx = jnp.split(proj, SPLIT_POINTS, axis=-1)
    heads = (b_sz, s_len, N_MLSTM_HEADS, MLSTM_HEAD_DIM)
    qf = q.astype(jnp.float32).reshape(heads) * (MLSTM_HEAD_DIM ** -0.5)
    kf = k.astype(jnp.float32).reshape(heads)
    vf = v.astype(jnp.float32).reshape(heads)
    log_i = ig.astype(jnp.float32)
    log_f = jax.nn.log_sigmoid(fg.astype(jnp.float32))
    h_m = mlstm_chunkwise(qf, kf, vf, log_i, log_f).reshape(b_sz, s_len, D_MLSTM)
    y_m = (jax.nn.sigmoid(o.astype(jnp.float32)) * h_m).astype(x.dtype)
    y_c = short_gated_conv(cb, cc, cx, conv_w)
    x = x + jnp.concatenate([y_m, y_c], axis=-1) @ w_out
    hn2 = rms_norm(x, norm_ffn)
    moe = hier_moe(hn2.reshape(b_sz * s_len, d), w_group, b_group, w_expert, b_expert,
                   w_gate, w_up, w_down)
    return x + moe.reshape(b_sz, s_len, d)

def setup_inputs(seed: int = 0) -> dict:
    key = jax.random.key(seed)
    ks = jax.random.split(key, 16)
    nrm = jax.random.normal
    x = nrm(ks[0], (BATCH, SEQ, D_MODEL), jnp.float32)
    norm_mix = 1.0 + 0.02 * nrm(ks[1], (DEPTH, D_MODEL), jnp.float32)
    w_in = nrm(ks[2], (DEPTH, D_MODEL, D_PROJ), jnp.float32) * (D_MODEL ** -0.5)
    b_in = 0.01 * nrm(ks[3], (DEPTH, D_PROJ), jnp.float32)
    b_in = b_in.at[:, F_OFF:F_OFF + N_MLSTM_HEADS].add(
        jnp.linspace(FORGET_BIAS_LO, FORGET_BIAS_HI, N_MLSTM_HEADS, dtype=jnp.float32))
    conv_w = nrm(ks[4], (DEPTH, CONV_WIDTH, D_CONV), jnp.float32) * (CONV_WIDTH ** -0.5)
    w_out = nrm(ks[5], (DEPTH, D_MIX, D_MODEL), jnp.float32) * (D_MIX ** -0.5)
    norm_ffn = 1.0 + 0.02 * nrm(ks[6], (DEPTH, D_MODEL), jnp.float32)
    w_group = nrm(ks[7], (DEPTH, D_MODEL, N_GROUPS), jnp.float32) * (D_MODEL ** -0.5)
    b_group = 0.01 * nrm(ks[8], (DEPTH, N_GROUPS), jnp.float32)
    w_expert = nrm(ks[9], (DEPTH, D_MODEL, N_EXPERTS), jnp.float32) * (D_MODEL ** -0.5)
    b_expert = 0.01 * nrm(ks[10], (DEPTH, N_EXPERTS), jnp.float32)
    w_gate = nrm(ks[11], (DEPTH, N_EXPERTS, D_MODEL, D_FF_EXPERT), jnp.float32) * (D_MODEL ** -0.5)
    w_up = nrm(ks[12], (DEPTH, N_EXPERTS, D_MODEL, D_FF_EXPERT), jnp.float32) * (D_MODEL ** -0.5)
    w_down = nrm(ks[13], (DEPTH, N_EXPERTS, D_FF_EXPERT, D_MODEL), jnp.float32) * (D_FF_EXPERT ** -0.5)
    norm_final = 1.0 + 0.02 * nrm(ks[14], (D_MODEL,), jnp.float32)
    return {
        'x': x, 'norm_mix': norm_mix, 'w_in': w_in, 'b_in': b_in, 'conv_w': conv_w,
        'w_out': w_out, 'norm_ffn': norm_ffn, 'w_group': w_group, 'b_group': b_group,
        'w_expert': w_expert, 'b_expert': b_expert, 'w_gate': w_gate, 'w_up': w_up,
        'w_down': w_down, 'norm_final': norm_final,
    }

def reference(x, norm_mix, w_in, b_in, conv_w, w_out, norm_ffn, w_group, b_group,
              w_expert, b_expert, w_gate, w_up, w_down, norm_final):
    for l in range(DEPTH):
        x = hybrid_layer(x, norm_mix[l], w_in[l], b_in[l], conv_w[l], w_out[l], norm_ffn[l],
                         w_group[l], b_group[l], w_expert[l], b_expert[l],
                         w_gate[l], w_up[l], w_down[l])
    return rms_norm(x, norm_final)


_drawn_inputs = setup_inputs


def setup_inputs(seed=0):
    import zlib

    import numpy as np

    out = dict(_drawn_inputs(seed))
    spreads = {}
    factors = {'b_group': 6.146, 'b_expert': 4.629, 'norm_final': 8.26, 'norm_ffn': 2.729}
    for name, (base, spread) in spreads.items():
        noise = np.random.default_rng([zlib.crc32(name.encode()), seed]).standard_normal(out[name].shape)
        drawn = base * np.exp(spread * noise) if base else spread * noise
        out[name] = jnp.asarray(drawn.astype(out[name].dtype))
    for name, factor in factors.items():
        out[name] = (out[name] * factor).astype(out[name].dtype)
    return out
```

```python
from contextlib import ExitStack

import concourse.bass as bass
from concourse import mybir

P = 128
F32 = mybir.dt.float32
I32 = mybir.dt.int32
ALU = mybir.AluOpType
ACT = mybir.ActivationFunctionType
AX = mybir.AxisListType

H = 4
CW = 3
NG, EG = 4, 8
CAP = 160
EPS = 1e-6
NEG = -1e30


def build(nc, x, norm_mix, w_in, b_in, conv_w, w_out, norm_ffn, w_group, b_group,
          w_expert, b_expert, w_gate, w_up, w_down, norm_final, out):
    _, S, D = x.shape
    NE, _, FF = w_gate.shape[1:]
    DM = D // 2
    DH = DM // H
    KT = D // P
    NTILE = S // P
    CT = 4
    TB = CT * P
    NB = S // TB
    MT = DM // P
    FT = FF // P
    GATES = 4 * DM
    CONV = GATES + 2 * H
    WC = 256
    SLOTS_B = 14
    E1 = DH + 1
    OVMAX = (2 * S) // CAP
    NW = NE + OVMAX
    NSLOT = (NW + 1) * CAP
    R1 = CAP - P
    NR = NG + NE
    QS = float(DH) ** -0.5
    assert DH == P and NSLOT % 80 == 0 and S % TB == 0 and NG * EG == NE and S // CAP < EG * 2

    xd = x.rearrange("b s d -> (b s) d")
    od = out.rearrange("b s d -> (b s) d")
    win = w_in[0].rearrange("(kt p) n -> p kt n", p=P)
    hn2_d = nc.dram_tensor("hn2_rows", (S, D), F32, kind="Internal").ap()
    x2_d = nc.dram_tensor("x2_rows", (S, D), F32, kind="Internal").ap()
    slot_d = nc.dram_tensor("slot_token", (NSLOT, 1), I32, kind="Internal").ap()
    y_d = nc.dram_tensor("y_rows", (NSLOT + CAP, D), F32, kind="Internal").ap()

    with ExitStack() as ctx:
        sems = {}

        def S_(name):
            if name not in sems:
                sems[name] = ctx.enter_context(nc.semaphore(name))
            return sems[name]

        def sb(name, shape, dt=F32):
            return ctx.enter_context(nc.sbuf_tensor(name, shape, dt))

        PROJ = ctx.enter_context(nc.psum_tensor("ps_proj", [P, 2, 512], F32))
        SC = ctx.enter_context(nc.psum_tensor("ps_scores", [P, 512], F32))
        RB = ctx.enter_context(nc.psum_tensor("ps_rows", [P, 512], F32))
        NUM = ctx.enter_context(nc.psum_tensor("ps_num", [P, 2, 512], F32))
        STA = ctx.enter_context(nc.psum_tensor("ps_state", [P, 2, 512], F32))
        NBANK = [SC, RB]

        NCOL = KT + 5 * MT + CW * MT
        by_row = sb("by_row", [NCOL, P])
        by_channel = sb("by_channel", [P, NCOL])
        gmix = by_channel[:, 0:KT]
        bcol = by_channel[:, KT:KT + 5 * MT].rearrange("p (i m) -> p i m", m=MT)
        cwc = by_channel[:, KT + 5 * MT:NCOL].rearrange("p (i m) -> p i m", m=MT)
        bvo = sb("bvo", [P, 2, DM])
        bgt = sb("bgt", [P, 2 * H])
        gffn = sb("gffn", [P, D])
        gfin = sb("gfin", [P, D])
        brt = sb("brt", [P, NR])
        wgt = sb("wgt", [P, KT, 2 * H])
        wrt = sb("wrt", [P, KT, NR])
        wo = sb("wo", [P, KT, D])
        ident = sb("ident", [P, P])
        cneg = sb("cneg", [P, P])
        upper = sb("upper", [P, P])
        ones = sb("ones", [P, P])
        sel = sb("sel", [H, H, P])
        cmask = sb("cmask", [H, TB])

        ww = [sb(f"ww{i}", [P, KT, WC]) for i in range(2)]
        xin = [sb(f"xin{i}", [P, D]) for i in range(2)]
        xn = [sb(f"xn{i}", [P, D]) for i in range(2)]
        st1 = sb("st1", [P, 2, 4])
        mhalf = sb("mhalf", [P, 1])
        st2 = sb("st2", [P, 2, 2])
        hnT = sb("hnT", [P, KT, TB])
        qT = sb("qT", [P, H, TB])
        kT = sb("kT", [P, H, TB])
        vx = sb("vx", [P, CT, H, E1])
        og = sb("og", [P, CT, DM])
        gt = sb("gt", [P, CT, 2 * H])
        cc = sb("cc", [P, 2, TB])
        uu = sb("uu", [P, MT, TB + 2])
        zz = sb("zz", [P, TB])
        yT = sb("yT", [P, KT, TB])
        mp = sb("mp", [H, CT + 1])
        dm = sb("dm", [H, CT])
        dg = sb("dg", [H, 2, CT, H])
        cols = sb("cols", [P, 3 * CT * H + 2 * CT * H])
        arg = sb("arg", [P, H, P])
        wint = sb("wint", [P, H, P])
        qw = sb("qw", [P, H, P])
        kw = sb("kw", [P, H, P])
        cst = sb("cst", [P, H, E1])
        den = sb("den", [P, 2, H])
        yn = sb("yn", [P, DM])
        xres = [sb(f"xres{i}", [P, D]) for i in range(2)]
        x2 = [sb(f"x2_{i}", [P, D]) for i in range(2)]
        hn2 = [sb(f"hn2_{i}", [P, D]) for i in range(2)]
        rows = [buf[0:H, j * TB:(j + 1) * TB] for buf in (*x2, *hn2) for j in range(2)]
        hn2T = sb("hn2T", [P, KT, P])
        lg = sb("lg", [P, NTILE, NR])

        NWS = KT // 2
        wgu = [wo[:, j, :].rearrange("p (a f) -> p a f", a=2) for j in range(KT)]
        wg, wu = wgu[:NWS], wgu[NWS:]
        wd = [b_[:, j * D:(j + 1) * D] for b_ in (og[:].rearrange("p t c -> p (t c)"),
                                                  vx[:].rearrange("p t h e -> p (t h e)")) for j in range(2)]
        assert D == 2 * FF and NWS + NWS == KT and FT == 4
        slot_i = sb("slot_i", [P, 2, NTILE], I32)
        slot_y = sb("slot_y", [P, 2, NTILE], I32)
        tok = sb("tok", [P, NTILE], I32)
        zero_f = sb("zero_f", [P, P])
        zero_i = sb("zero_i", [80, NSLOT // 80], I32)
        order = sb("order", [P, EG])
        eidx = sb("eidx", [P, NE])
        ksteps = sb("ksteps", [P, 2 * EG])
        item_n = sb("item_n", [P, OVMAX + 1])
        tw = sb("tw", [P, 2, NTILE])
        item_e = sb("item_e", [P, NW + 1], I32)
        n_items = sb("n_items", [P, 1], I32)
        xg = xn[0]
        xg1 = xn[1]
        xT = hnT[:].rearrange("p k t -> p (k t)")[:, 0:KT * CAP].rearrange("p (k t) -> p k t", k=KT)
        sgt = qT[:].rearrange("p k t -> p (k t)")[:, 0:FT * CAP].rearrange("p (k t) -> p k t", k=FT)
        hT = kT[:].rearrange("p k t -> p (k t)")[:, 0:FT * CAP].rearrange("p (k t) -> p k t", k=FT)
        ydT = yT[:].rearrange("p k t -> p (k t)")[:, 0:KT * CAP].rearrange("p (k t) -> p k t", k=KT)
        yr = xin[0]
        yr1 = xin[1]
        idx = sb("idx", [P, 2], I32)
        yg = [[wo[:, 2 * j + i, :] for i in range(2)] for j in range(2)]
        routing = ww[0][:].rearrange("p k n -> p (k n)")
        routing1 = ww[1][:].rearrange("p k n -> p (k n)")

        uses = []
        for h in range(H):
            uses.append(("q", "D", h))
        for h in range(H):
            uses.append(("k", "A", h))
        for s in range(2):
            for t in range(CT):
                uses.append(("v", "D", (s, t)))
        uses.append(("g", "D", 0))
        for s in range(2):
            for t in range(CT):
                uses.append(("o", "D", (s, t)))
        for s in range(2):
            for i in range(2):
                uses.append(("cc", "A", 2 * s + i))
            for i in range(2):
                uses.append(("cx", "D", 2 * s + i))
            for i in range(2):
                uses.append(("cb", "D", 2 * s + i))
        for t in range(CT):
            for half in range(2):
                uses.append(("w", "D", (t, half)))
        NU = len(uses)
        NUD = sum(u[1] == "D" for u in uses)
        NUA = NU - NUD
        number = {(u[0], u[2]): n for n, u in enumerate(uses)}

        def emptied(n):
            e = uses[n][1]
            before = sum(u[1] == e for u in uses[:n + 1])
            return (S_("bank_emptied_dve"), before, NUD) if e == "D" else (S_("bank_emptied_act"), before, NUA)

        slot_last = [number[u] for u in (("q", 1), ("q", 3), ("k", 1), ("k", 3), ("v", (0, CT - 1)),
                                         ("v", (1, CT - 1)), ("o", (0, CT - 1)), ("o", (1, CT - 1)),
                                         ("cc", 1), ("cx", 1), ("cb", 1), ("cc", 3), ("cx", 3), ("cb", 3))]
        NCONST = 10
        slot_cols = [0, WC, DM, DM + WC, 2 * DM, 2 * DM + WC, 3 * DM, 3 * DM + WC]
        for s in range(2):
            slot_cols += [CONV + DM + s * WC, CONV + 2 * DM + s * WC, CONV + s * WC]
        assert len(slot_cols) == SLOTS_B

        def own_instruction(eng):
            eng.sem_inc(S_("waits_done"), 1)

        def x2f(g):
            return hn2[g % 2][:]

        block = ctx.enter_context(nc.Block())

        @block.sync
        def _(sp):
            def load_x(b, t):
                row = (b * CT + t) * P
                if not isinstance(b, int):
                    row = nc.s_assert_within(row, TB, S - P)
                sp.dma_start(xin[t % 2][:], xd[bass.ds(row, P)]).then_inc(S_(f"x_loaded{t % 2}"), 16)

            def load_xres(b, t):
                sp.dma_start(xres[t % 2][:], xd[bass.ds((b * CT + t) * P, P)]).then_inc(
                    S_(f"xres_loaded{t % 2}"), 16)

            def load_w(n):
                c = slot_cols[n]
                sp.dma_start(ww[n % 2][:], win[:, :, c:c + WC]).then_inc(S_(f"w_loaded{n % 2}"), 16)

            load_x(0, 0)
            load_x(0, 1)
            c1 = S_("consts_loaded")
            rl = S_("by_row_loaded")
            bi = b_in[0]
            sp.dma_start(by_row[0:KT], norm_mix[0].rearrange("(k p) -> k p", p=P)).then_inc(rl, 16)
            for i, c in enumerate((0, DM, CONV, CONV + DM, CONV + 2 * DM)):
                o = KT + i * MT
                sp.dma_start(by_row[o:o + MT], bi[c:c + DM].rearrange("(m p) -> m p", p=P)).then_inc(rl, 16)
            sp.dma_start(by_row[NCOL - CW * MT:NCOL], conv_w[0].rearrange("j (m p) -> (j m) p", p=P)
                         ).then_inc(rl, 16)
            load_w(0)
            load_w(1)
            for j in range(2):
                c = (2 + j) * DM
                sp.dma_start(bvo[:, j], bi[c:c + DM].partition_broadcast(P)).then_inc(c1, 16)
            sp.dma_start(bgt[:], bi[GATES:GATES + 2 * H].partition_broadcast(P)).then_inc(c1, 16)
            sp.dma_start(wgt[:], win[:, :, GATES:GATES + 2 * H]).then_inc(c1, 16)
            sp.dma_start(gffn[:], norm_ffn[0].partition_broadcast(P)).then_inc(c1, 16)
            sp.dma_start(gfin[:], norm_final.partition_broadcast(P)).then_inc(c1, 16)
            sp.dma_start(brt[:, 0:NG], b_group[0].partition_broadcast(P)).then_inc(c1, 16)
            sp.dma_start(brt[:, NG:NR], b_expert[0].partition_broadcast(P)).then_inc(c1, 16)
            sp.dma_start(wrt[:, :, 0:NG], w_group[0].rearrange("(k p) n -> p k n", p=P)).then_inc(c1, 16)
            sp.dma_start(wrt[:, :, NG:NR], w_expert[0].rearrange("(k p) n -> p k n", p=P)).then_inc(c1, 16)
            for t in range(2, CT):
                sp.wait_ge(S_("xn_ready"), t - 1)
                load_x(0, t)
            sp.dma_start(wo[:], w_out[0].rearrange("(k p) n -> p k n", p=P)).then_inc(S_("wo_loaded"), 16)
            with sp.Fori(0, NB) as b:
                for n in range(2, SLOTS_B):
                    sp.wait_ge(S_("proj_done"), b * NU + slot_last[n - 2] + 1)
                    load_w(n)
                for t in range(CT):
                    if t < 2:
                        sp.wait_ge(S_("bank_emptied_dve"), b * NUD)
                    else:
                        n = number[("w", (t - 2, 1))]
                        s, k, per = emptied(n)
                        sp.wait_ge(s, b * per + k)
                    load_xres(b, t)
                    with sp.If(b < NB - 1):
                        sp.wait_ge(S_("xn_ready"), (b + 1) * CT + t - 1)
                        load_x(b + 1, t)
                    if t < 2:
                        with sp.If(b < NB - 1):
                            sp.wait_ge(S_("proj_done"), b * NU + slot_last[SLOTS_B - 2 + t] + 1)
                            load_w(t)

            def expert_weights(e, first, k):
                for j in range(NWS):
                    if not first:
                        sp.wait_ge(S_("we_used"), (k - 1) * (NWS + FT) + j + 1)
                    src = w_gate[0][bass.ds(e, 1), 2 * j * P:(2 * j + 2) * P]
                    sp.dma_start(wg[j], src.rearrange("o (k p) n -> p (o k) n", p=P)).then_inc(
                        S_(f"wgu_loaded{j}"), 16)
                    src = w_up[0][bass.ds(e, 1), 2 * j * P:(2 * j + 2) * P]
                    sp.dma_start(wu[j], src.rearrange("o (k p) n -> p (o k) n", p=P)).then_inc(
                        S_(f"wgu_loaded{j}"), 16)
                for f in range(FT):
                    if not first:
                        sp.wait_ge(S_("we_used"), (k - 1) * (NWS + FT) + NWS + f + 1)
                    src = w_down[0][bass.ds(e, 1), f * P:(f + 1) * P]
                    sp.dma_start(wd[f], src.rearrange("o p n -> p (o n)")).then_inc(
                        S_(f"wd_loaded{f}"), 16)

            sp.wait_ge(S_("logits_emptied"), NTILE)
            expert_weights(0, True, 0)
            sp.wait_ge(S_("routed"), 1)
            n = sp.value_load(n_items[0:1, 0:1], min_val=NE, max_val=NW)
            with sp.Fori(1, NW) as k:
                with sp.If(k < n):
                    e = sp.value_load(item_e[0:1, bass.ds(k, 1)], min_val=0, max_val=NE - 1)
                    expert_weights(e, False, k)

            for g in range(NTILE):
                if g < 2:
                    sp.wait_ge(S_(f"x2_stored{0}"), 16 * NTILE // 2)
                    sp.wait_ge(S_(f"x2_stored{1}"), 16 * NTILE // 2)
                if g >= 2:
                    sp.wait_ge(S_("moe_added"), g - 1)
                sp.dma_start(x2[g % 2][:], x2_d[g * P:(g + 1) * P]).then_inc(S_(f"x2_back{g % 2}"), 16)
                if g >= 1:
                    sp.wait_ge(S_("out_ready"), g)
                    sp.dma_start(od[(g - 1) * P:g * P], xres[(g - 1) % 2][:]).then_inc(
                        S_(f"out_stored{(g - 1) % 2}"), 16)
            g = NTILE
            sp.wait_ge(S_("out_ready"), g)
            sp.dma_start(od[(g - 1) * P:g * P], xres[(g - 1) % 2][:]).then_inc(
                S_(f"out_stored{(g - 1) % 2}"), 16)
            for i in range(2):
                sp.wait_ge(S_(f"out_stored{i}"), 16 * NTILE // 2)

        @block.tensor
        def _(pe):
            def bank_free(b, n):
                if n == 0:
                    s, k, per = emptied(NU - 1)
                    pe.wait_ge(s, b * per)
                    pe.wait_ge(S_("bank_emptied_act"), b * NUA)
                elif n == 1:
                    pe.wait_ge(S_("bank_emptied_dve"), b * NUD)
                else:
                    s, k, per = emptied(n - 2)
                    pe.wait_ge(s, b * per + k)

            def w_here(b, n):
                pe.wait_ge(S_(f"w_loaded{n % 2}"), (b * (SLOTS_B // 2) + n // 2 + 1) * 16)

            def channels_out(b, kind, m, slot, first):
                n = number[(kind, m)]
                if first:
                    w_here(b, slot)
                bank_free(b, n)
                c = (m % 2) * P
                for k in range(KT):
                    mm = pe.matmul(PROJ[:, n % 2, :], ww[slot % 2][:, k, c:c + P], hnT[:, k, :],
                                   start=(k == 0), stop=(k == KT - 1))
                mm.then_inc(S_("proj_done"), 1)

            def tokens_out(b, kind, s, t, slot, first):
                n = number[(kind, (s, t))]
                if first:
                    w_here(b, slot)
                bank_free(b, n)
                for k in range(KT):
                    mm = pe.matmul(PROJ[:, n % 2, 0:WC], hnT[:, k, t * P:(t + 1) * P], ww[slot % 2][:, k, :],
                                   start=(k == 0), stop=(k == KT - 1))
                mm.then_inc(S_("proj_done"), 1)

            def norm_transposes(g, t, waits):
                pe.wait_ge(S_("xn_ready"), g + 1)
                for half in range(2):
                    waits(half)
                    for i in range(4):
                        k = 4 * half + i
                        mm = pe.transpose(NBANK[half][:, i * P:(i + 1) * P], xn[t % 2][:, k * P:(k + 1) * P],
                                          ident[:])
                    mm.then_inc(S_("nT_done"), 1)

            pe.wait_ge(S_("masks_ready"), 1)
            pe.wait_ge(S_("by_row_loaded"), 16 * 7)
            pe.transpose(PROJ[:, 0, 0:NCOL], by_row[:], ident[0:NCOL, 0:NCOL]).then_inc(S_("by_channel_done"), 1)
            for t in range(CT):
                def waits(half, t=t):
                    if t > 0:
                        pe.wait_ge(S_("hnT_ready"), 2 * (t - 1) + half + 1)
                norm_transposes(t, t, waits)

            with pe.Fori(0, NB) as b:
                pe.wait_ge(S_("hnT_ready"), (b + 1) * 2 * CT)
                for kind, base in (("q", 0), ("k", 2)):
                    for m in range(H):
                        channels_out(b, kind, m, base + m // 2, m % 2 == 0)
                for s in range(2):
                    for t in range(CT):
                        tokens_out(b, "v", s, t, 4 + s, t == 0)
                n = number[("g", 0)]
                if True:
                    pe.wait_ge(S_("consts_loaded"), 16 * NCONST)
                    bank_free(b, n)
                    for t in range(CT):
                        for k in range(KT):
                            mm = pe.matmul(PROJ[:, n % 2, t * 8:t * 8 + 2 * H], hnT[:, k, t * P:(t + 1) * P],
                                           wgt[:, k, :], start=(k == 0), stop=(k == KT - 1))
                    mm.then_inc(S_("proj_done"), 1)
                for t in range(CT):
                    tokens_out(b, "o", 0, t, 6, t == 0)
                s, k_, per = emptied(n)
                pe.wait_ge(s, b * per + k_)
                for j, bank in enumerate((SC, RB)):
                    for t in range(CT):
                        mm = pe.transpose(bank[0:H, t * P:(t + 1) * P], gt[:, t, j * H:(j + 1) * H], ident[:])
                    mm.then_inc(S_("gateT_done"), 1)
                for t in range(CT):
                    tokens_out(b, "o", 1, t, 7, t == 0)
                pe.wait_ge(S_("logits_emptied"), b * CT)
                pe.wait_ge(S_("rows_a_ready"), b + 1)
                pe.wait_ge(S_("rows_exp_ready"), 2 * (b + 1))
                pe.wait_ge(S_("diag_ready"), b + 1)
                own_instruction(pe)
                for j, r in enumerate((2, 5, 6)):
                    for c in range(CT):
                        o = (j * CT + c) * H
                        pe.transpose(STA[:, 0, o:o + H], rows[r][:, c * P:(c + 1) * P], ident[0:H, 0:H])
                o = 3 * CT * H
                pe.matmul(STA[:, 0, o:o + 2 * CT * H], ones[0:H, :], dg[:].rearrange("h a c g -> h (a c g)"),
                          start=True, stop=True).then_inc(S_("cols_done"), 1)

                conv = [(k, 2 * s + i, 8 + 3 * s + j, i == 0) for s in range(2)
                        for j, k in enumerate(("cc", "cx", "cb")) for i in range(2)]

                def conv_products(i):
                    kind, m, slot, first = conv[i]
                    channels_out(b, kind, m, slot, first)

                for c in range(CT):
                    q = b * CT + c
                    cs = slice(c * P, (c + 1) * P)
                    if c == 0:
                        s, k_, per = emptied(number[("k", H - 1)])
                        pe.wait_ge(s, b * per + k_)
                    pe.wait_ge(S_("state_ready"), q + 1)
                    for h in range(H):
                        mm = pe.transpose(STA[:, 1, h * P:(h + 1) * P], kT[:, h, cs], ident[:])
                    mm.then_inc(S_("kT_done"), 1)
                    if c == 0:
                        pe.wait_ge(S_("rows_exp_ready"), 2 * (b + 1))
                    else:
                        pe.wait_ge(S_("probs_ready"), q)
                        pe.wait_ge(S_("yT_ready"), q)
                    for h in range(H):
                        mm = pe.matmul(SC[:, h * P:(h + 1) * P], kT[:, h, cs], qT[:, h, cs], start=True, stop=True)
                    for h in range(H):
                        mm = pe.matmul(RB[:, h * P:(h + 1) * P], sel[:, h, :], rows[3][:, cs], start=True, stop=True)
                    mm.then_inc(S_("scores_done"), 1)
                    conv_products(3 * c)
                    pe.wait_ge(S_("probs_ready"), q + 1)
                    pe.wait_ge(S_("qw_ready"), q + 1)
                    if c == 0:
                        pe.wait_ge(S_("hn2T_ready"), b * 2 * CT)
                    else:
                        pe.wait_ge(S_("yn_ready"), q)
                    for h in range(H):
                        o = NUM[:, h // 2, (h % 2) * E1:(h % 2 + 1) * E1]
                        pe.matmul(o, arg[:, h, :], vx[:, c, h, :], start=True, stop=False)
                        mm = pe.matmul(o, qw[:, h, :], cst[:, h, :], start=False, stop=True)
                    mm.then_inc(S_("num_done"), 1)
                    pe.wait_ge(S_("kw_ready"), q + 1)
                    for h in range(H):
                        o = STA[:, h // 2, (h % 2) * E1:(h % 2 + 1) * E1]
                        mm = pe.matmul(o, kw[:, h, :], vx[:, c, h, :], start=True, stop=True)
                    mm.then_inc(S_("update_done"), 1)
                    conv_products(3 * c + 1)
                    pe.wait_ge(S_("yn_ready"), q + 1)
                    for h in range(H):
                        mm = pe.transpose(RB[:, h * P:(h + 1) * P], yn[:, h * P:(h + 1) * P], ident[:])
                    mm.then_inc(S_("ynT_done"), 1)
                    conv_products(3 * c + 2)

                def router(t):
                    g = b * CT + t
                    pe.wait_ge(S_("hn2_ready"), g + 1)
                    for half in range(2):
                        if t > 0:
                            pe.wait_ge(S_("hn2T_ready"), 2 * (g - 1) + half + 1)
                        for i in range(4):
                            k = 4 * half + i
                            mm = pe.transpose(NUM[:, half, i * P:(i + 1) * P], hn2[t % 2][:, k * P:(k + 1) * P],
                                              ident[:])
                        mm.then_inc(S_("hn2T_done"), 1)
                    pe.wait_ge(S_("hn2T_ready"), 2 * g + 2)
                    if t > 0:
                        pe.wait_ge(S_("logits_emptied"), g)
                    for k in range(KT):
                        mm = pe.matmul(STA[:, 0, 0:NR], hn2T[:, k, :], wrt[:, k, :], start=(k == 0),
                                       stop=(k == KT - 1))
                    mm.then_inc(S_("logits_done"), 1)

                pe.wait_ge(S_("wo_loaded"), 16)
                s, k_, per = emptied(number[("cb", MT - 1)])
                pe.wait_ge(s, b * per + k_)
                pe.wait_ge(S_("state_ready"), (b + 1) * CT + 1)
                pe.wait_ge(S_("yT_ready"), (b + 1) * CT)
                for t in range(CT):
                    for half in range(2):
                        n = number[("w", (t, half))]
                        bank_free(b, n)
                        for k in range(KT):
                            mm = pe.matmul(PROJ[:, n % 2, :], yT[:, k, t * P:(t + 1) * P],
                                           wo[:, k, half * 512:(half + 1) * 512], start=(k == 0), stop=(k == KT - 1))
                        mm.then_inc(S_("proj_done"), 1)

                    with pe.If(b < NB - 1):
                        def waits(half, t=t):
                            if t > 0:
                                pe.wait_ge(S_("hnT_ready"), (b + 1) * 2 * CT + 2 * (t - 1) + half + 1)
                        norm_transposes((b + 1) * CT + t, t, waits)
                    if t > 0:
                        router(t - 1)
                router(CT - 1)

            mask = routing1[:, 0:NTILE * NE]
            pe.wait_ge(S_("mask_ready"), 1)
            pe.matmul(SC[:], upper[:], mask, start=True, stop=True)
            pe.matmul(RB[:], ones[:], mask, start=True, stop=True).then_inc(S_("ranks_done"), 1)

            GU = [PROJ[:, 0, :], PROJ[:, 1, :], SC[:], RB[:]]
            DN = [STA[:, 1, :], NUM[:, 0, :], NUM[:, 1, :], STA[:, 0, :]]
            XB = [NUM[:, 0, :], NUM[:, 1, :], STA[:, 0, :]]

            def x_transposes(k):
                pe.wait_ge(S_("x_gathered"), (k + 1) * 16)
                pe.wait_ge(S_("x1_gathered"), (k + 1) * 16)
                for kt in range(KT):
                    o = XB[kt // 3][:, (kt % 3) * CAP:(kt % 3 + 1) * CAP]
                    pe.transpose(o[:, 0:P], xg[:, kt * P:(kt + 1) * P], ident[:])
                    mm = pe.transpose(o[:, P:CAP], xg1[0:R1, kt * P:(kt + 1) * P], ident[0:R1, 0:R1])
                    if kt % 3 == 2 or kt == KT - 1:
                        mm.then_inc(S_("xT_done"), 1)

            def y_transposes(k):
                pe.wait_ge(S_("yd_ready"), k * 4)
                for kt in range(KT):
                    pe.transpose(NUM[:, kt // 4, (kt % 4) * P:(kt % 4 + 1) * P], ydT[:, kt, 0:P], ident[:])
                    mm = pe.transpose(STA[0:R1, kt // 4, (kt % 4) * P:(kt % 4 + 1) * P], ydT[:, kt, P:CAP], ident[:])
                mm.then_inc(S_("yrT_done"), 1)

            pe.wait_ge(S_("routed"), 1)
            n = pe.value_load(n_items[0:1, 0:1], min_val=NE, max_val=NW)
            x_transposes(0)
            with pe.Fori(0, NW) as k:
                with pe.If(k < n):
                    pe.wait_ge(S_("xT_ready"), (k + 1) * 3)
                    pe.wait_ge(S_("hid_ready"), k * 2)
                    for kt in range(KT):
                        j = kt // 2
                        if kt % 2 == 0:
                            pe.wait_ge(S_(f"wgu_loaded{j}"), (k + 1) * 32)
                        if kt == KT // 2:
                            y_transposes(k)
                        for m in range(FT):
                            pe.matmul(GU[m][:, 0:CAP], wg[j][:, kt % 2, m * P:(m + 1) * P], xT[:, kt, :],
                                      start=(kt == 0), stop=(kt == KT - 1), skip_group_check=True)
                            mm = pe.matmul(GU[m][:, CAP:2 * CAP], wu[j][:, kt % 2, m * P:(m + 1) * P], xT[:, kt, :],
                                           start=False, stop=(kt == KT - 1), skip_group_check=True)
                            if m == FT - 1 and kt % 2 == 1:
                                mm.then_inc(S_("we_used"), 1)
                    pe.wait_ge(S_("yr_ready"), 2 * (k + 1))
                    x_transposes(k + 1)
                    pe.wait_ge(S_("hid_ready"), 2 * (k + 1))
                    for i in range(KT):
                        bank, o = DN[i // 2], (i % 2) * CAP
                        if i == 2:
                            pe.wait_ge(S_("xT_ready"), (k + 2) * 3)
                        for f in range(FT):
                            if i == 0:
                                pe.wait_ge(S_(f"wd_loaded{f}"), (k + 1) * 16)
                            mm = pe.matmul(bank[:, o:o + CAP], wd[f][:, i * P:(i + 1) * P], hT[:, f, :],
                                           start=(f == 0), stop=(f == FT - 1))
                            if i == KT - 1:
                                mm.then_inc(S_("we_used"), 1)
                        if i % 2 == 1 and i < KT - 1:
                            mm.then_inc(S_("dn_done"), 1)
            y_transposes(n)

        @block.scalar
        def _(act):
            def norm_tile(g, t, slot_count):
                act.wait_ge(S_(f"x_loaded{t % 2}"), 16 * slot_count)
                yield_free(g)
                act.activation(xn[t % 2][:], xin[t % 2][:], ACT.Square,
                               accum_out=st1[:, t % 2, 0:1]).then_inc(S_("ss_ready"), 1)
                act.wait_ge(S_("rs_ready"), g + 1)
                act.activation(xn[t % 2][:], xin[t % 2][:], ACT.Copy,
                               scale=st1[:, t % 2, 2:3]).then_inc(S_("xn_ready"), 1)

            def yield_free(g):
                if not isinstance(g, int) or g >= 2:
                    act.wait_ge(S_("nT_done"), 2 * (g - 1))

            for t in range(CT):
                norm_tile(t, t, t // 2 + 1)
            act.wait_ge(S_("by_channel_ready"), 1)
            with act.Fori(0, NB) as b:
                for m in range(H):
                    n = number[("k", m)]
                    act.wait_ge(S_("proj_done"), b * NU + n + 1)
                    act.activation(kT[:, m, :], PROJ[:, n % 2, :], ACT.Identity,
                                   bias=bcol[:, 1, m:m + 1]).then_inc(S_("bank_emptied_act"), 1)
                n = number[("g", 0)]

                def exp_o(s):
                    for t in range(CT):
                        sm, k_, per = emptied(number[("o", (s, t))])
                        act.wait_ge(sm, b * per + k_)
                        act.activation(og[:, t, s * WC:(s + 1) * WC], og[:, t, s * WC:(s + 1) * WC], ACT.Exp,
                                       scale=-1.0).then_inc(S_("exp_o_ready"), 1)

                exp_o(0)
                act.wait_ge(S_("gateT_done"), 2 * b + 2)
                for i in range(2):
                    act.wait_ge(S_(f"x2_stored{i}"), 32 * b)
                    act.wait_ge(S_(f"hn2_stored{i}"), 32 * b)
                act.activation(rows[4][:, :], RB[0:H, :], ACT.Abs).then_inc(S_("soft_step"), 1)
                act.wait_ge(S_("soft_step"), 3 * b + 1)
                act.activation(rows[5][:, :], rows[4][:, :], ACT.Exp, scale=-1.0).then_inc(S_("soft_step"), 1)
                act.wait_ge(S_("soft_step"), 3 * b + 2)
                act.activation(rows[6][:, :], rows[5][:, :], ACT.Ln, bias=1.0).then_inc(S_("soft_step"), 1)
                act.wait_ge(S_("rows_m_ready"), b + 1)
                act.activation(rows[6][:, :], rows[1][:, :], ACT.Exp, scale=-1.0).then_inc(S_("rows_exp_ready"), 1)
                act.wait_ge(S_("dm_ready"), b + 1)
                act.activation(dm[:], dm[:], ACT.Exp).then_inc(S_("decay_ready"), 1)
                act.wait_ge(S_("rows_w_ready"), b + 1)
                act.activation(rows[5][:, :], rows[4][:, :], ACT.Exp).then_inc(S_("rows_exp_ready"), 1)
                exp_o(1)
                act.wait_ge(S_("cols_ready"), b + 1)
                WCOL, ACOL, MCOL = CT * H, 0, 4 * CT * H

                def conv_act(i):
                    if i in (0, 1, 6, 7):
                        m = i if i < 2 else i - 4
                        n = number[("cc", m)]
                        act.wait_ge(S_("proj_done"), b * NU + n + 1)
                        if m >= 2:
                            sm, k_, per = emptied(number[("cx", m - 2)])
                            act.wait_ge(sm, b * per + k_)
                        else:
                            act.wait_ge(S_("bank_emptied_dve"), b * NUD)
                        act.activation(cc[:, m % 2, :], PROJ[:, n % 2, :], ACT.Identity,
                                       bias=bcol[:, 3, m:m + 1]).then_inc(S_("bank_emptied_act"), 1)

                for c in range(CT):
                    q = b * CT + c
                    act.wait_ge(S_("kT_done"), q + 1)
                    for h in range(H):
                        i_ = act.activation(kw[:, h, :], STA[:, 1, h * P:(h + 1) * P], ACT.Copy,
                                            scale=cols[:, WCOL + c * H + h:WCOL + c * H + h + 1])
                    i_.then_inc(S_("kw_ready"), 1)
                    act.wait_ge(S_("arg_ready"), q + 1)
                    for h in range(H):
                        o = MCOL + c * H + h
                        i_ = act.activation(wint[:, h, :], RB[:, h * P:(h + 1) * P], ACT.Exp, bias=cols[:, o:o + 1])
                    i_.then_inc(S_("wint_ready"), 1)
                    for h in range(H):
                        o = ACOL + c * H + h
                        i_ = act.activation(arg[:, h, :], arg[:, h, :], ACT.Exp, bias=cols[:, o:o + 1])
                    i_.then_inc(S_("decays_ready"), 1)
                    conv_act(3 * c)
                    conv_act(3 * c + 1)
                    act.wait_ge(S_("ynT_done"), q + 1)
                    act.activation(yT[:, 0:H, c * P:(c + 1) * P], RB[:].rearrange("p (h t) -> p h t", h=H),
                                   ACT.Copy).then_inc(S_("yT_ready"), 1)
                    conv_act(3 * c + 2)

                def router_act(t):
                    g = b * CT + t
                    for half in range(2):
                        act.wait_ge(S_("hn2T_done"), 2 * g + half + 1)
                        act.activation(hn2T[:, 4 * half:4 * half + 4, :],
                                       NUM[:, half, :].rearrange("p (k t) -> p k t", k=4),
                                       ACT.Copy).then_inc(S_("hn2T_ready"), 1)

                for t in range(CT):
                    g = b * CT + t
                    n = number[("w", (t, 1))]
                    s, k_, per = emptied(n)
                    act.wait_ge(s, b * per + k_)
                    if t >= 2:
                        act.wait_ge(S_(f"hn2_stored{t % 2}"), 16 * (2 * b + t // 2))
                        act.wait_ge(S_("hn2T_done"), 2 * (g - 1))
                    else:
                        act.wait_ge(S_(f"hn2_stored{t % 2}"), 32 * b)
                        act.wait_ge(S_("hn2T_done"), 2 * CT * b)
                    act.activation(hn2[t % 2][:], x2[t % 2][:], ACT.Square,
                                   accum_out=st1[:, t % 2, 3:4]).then_inc(S_("ss2_ready"), 1)
                    with act.If(b < NB - 1):
                        norm_tile((b + 1) * CT + t, t, (b + 1) * 2 + t // 2 + 1)
                    act.wait_ge(S_("hn2_ready"), g + 1)
                    act.dma_start(hn2_d[bass.ds(g * P, P)], hn2[t % 2][:]).then_inc(S_(f"hn2_stored{t % 2}"), 16)
                    act.dma_start(x2_d[bass.ds(g * P, P)], x2[t % 2][:]).then_inc(S_(f"x2_stored{t % 2}"), 16)
                    if t > 0:
                        router_act(t - 1)
                router_act(CT - 1)

            ex = routing[:, 0:(NG + 1) * NTILE].rearrange("p (t n) -> p t n", n=NG + 1)
            act.wait_ge(S_("route_exp_in"), 1)
            act.activation(ex, ex, ACT.Exp).then_inc(S_("route_exp"), 1)

            act.wait_ge(S_("routed"), 1)
            n = act.value_load(n_items[0:1, 0:1], min_val=NE, max_val=NW)
            XB = [NUM[:, 0, :], NUM[:, 1, :], STA[:, 0, :]]
            DN = [STA[:, 1, :], NUM[:, 0, :], NUM[:, 1, :], STA[:, 0, :]]

            def x_turned(k):
                for i in range(3):
                    w = min(3, KT - 3 * i)
                    act.wait_ge(S_("xT_done"), k * 3 + i + 1)
                    act.activation(xT[:, 3 * i:3 * i + w, :], XB[i][:, 0:w * CAP].rearrange("p (k t) -> p k t", k=w),
                                   ACT.Copy).then_inc(S_("xT_ready"), 1)

            def y_turned(k):
                act.wait_ge(S_("yrT_done"), k + 1)
                act.wait_ge(S_("y_stored"), 16 * k)
                act.activation(yr[:], NUM[:].rearrange("p a t -> p (a t)"), ACT.Copy).then_inc(S_("yr_ready"), 1)

            x_turned(0)
            with act.Fori(0, NW) as k:
                with act.If(k < n):
                    y_turned(k)
                    for half in range(2):
                        act.wait_ge(S_("we_used"), k * (NWS + FT) + NWS)
                        for m in (2 * half, 2 * half + 1):
                            src = [PROJ[:, 0, :], PROJ[:, 1, :], SC[:], RB[:]][m]
                            i_ = act.activation(sgt[:, m, :], src[:, 0:CAP], ACT.Silu)
                        i_.then_inc(S_("silu_ready"), 1)
                    x_turned(k + 1)
                    for i in range(2):
                        act.wait_ge(S_("dn_done"), k * 3 + i + 1)
                        act.activation(ydT[:, 2 * i:2 * i + 2, :],
                                       DN[i][:, 0:2 * CAP].rearrange("p (k t) -> p k t", k=2),
                                       ACT.Copy).then_inc(S_("yd_ready"), 1)
            y_turned(n)

            for g in range(NTILE):
                act.wait_ge(S_("moe_added"), g + 1)
                if g >= 2:
                    act.wait_ge(S_(f"out_stored{g % 2}"), 16 * (g // 2))
                act.activation(xres[g % 2][:], x2f(g), ACT.Square,
                               accum_out=st1[:, g % 2, 0:1]).then_inc(S_("ss3_ready"), 1)

        @block.gpsimd
        def _(pool):
            m = S_("mask_step")
            pool.memset(ident[:], 0.0).then_inc(m, 1)
            pool.memset(cneg[:], 0.0).then_inc(m, 1)
            pool.memset(upper[:], 1.0).then_inc(m, 1)
            pool.memset(ones[:], 1.0).then_inc(m, 1)
            pool.memset(sel[:], 0.0).then_inc(m, 1)
            pool.memset(cmask[:], 1.0).then_inc(m, 1)
            pool.memset(uu[:], 0.0).then_inc(m, 1)
            pool.memset(cst[:], 0.0).then_inc(m, 1)
            pool.memset(vx[:, :, :, DH:E1], 1.0).then_inc(m, 1)
            pool.memset(mp[:], 0.0).then_inc(m, 1)
            pool.memset(mhalf[:], -0.5).then_inc(m, 1)
            pool.wait_ge(m, 11)
            pool.affine_select(out=ident[:], in_=ident[:], compare_op=ALU.not_equal, fill=1.0, base=0,
                               pattern=[[-1, P]], channel_multiplier=1).then_inc(m, 1)
            pool.affine_select(out=cneg[:], in_=cneg[:], compare_op=ALU.is_ge, fill=NEG, base=0,
                               pattern=[[1, P]], channel_multiplier=-1).then_inc(m, 1)
            pool.affine_select(out=upper[:], in_=upper[:], compare_op=ALU.is_gt, fill=0.0, base=0,
                               pattern=[[1, P]], channel_multiplier=-1).then_inc(m, 1)
            pool.affine_select(out=sel[:], in_=sel[:], compare_op=ALU.not_equal, fill=1.0, base=0,
                               pattern=[[-1, H], [0, P]], channel_multiplier=1).then_inc(m, 1)
            pool.memset(cmask[:].rearrange("h (c t) -> h c t", c=CT)[:, :, 0:1], 0.0).then_inc(m, 1)
            pool.wait_ge(m, 16)
            pool.sem_inc(S_("masks_ready"), 1)
            rc = S_("route_consts")
            for tile, step, base in ((order, -1, EG), (eidx, 1, 0), (ksteps, CAP, CAP), (item_n, 1, 0)):
                pool.iota(tile[:], pattern=[[step, tile.shape[1]]], base=base, channel_multiplier=0,
                          allow_small_or_imprecise_dtypes=True).then_inc(rc, 1)
            pool.iota(tok[:], pattern=[[P, NTILE]], base=0, channel_multiplier=1).then_inc(rc, 1)
            pool.memset(zero_i[:], 0).then_inc(rc, 1)
            pool.memset(zero_f[:], 0.0).then_inc(rc, 1)
            pool.wait_ge(rc, 7)
            spare = y_d[(NE + 1) * CAP:NSLOT + CAP].rearrange("(p r) d -> p (r d)", p=80)
            step = 4 * D
            with pool.Fori(0, spare.shape[1] // step) as i:
                pool.dma_start(spare[:, bass.ds(i * step, step)].rearrange("p (a c) -> p a c", c=P),
                               zero_f[0:80].unsqueeze(1).broadcast_to([80, step // P, P])
                               ).then_inc(S_("spare_cleared"), 16)
            pool.dma_start(slot_d.rearrange("(p n) o -> p (n o)", n=NSLOT // 80), zero_i[:]).then_inc(
                S_("slots_cleared"), 16)

            def rsqrt(wait_sem, value, slot, col, name, count):
                pool.wait_ge(S_(wait_sem), value)
                own_instruction(pool)
                pool.tensor_scalar(st1[:, slot, 1:2], st1[:, slot, col:col + 1], 1.0 / D, EPS, ALU.mult,
                                   ALU.add).then_inc(S_("ms_ready"), 1)
                pool.wait_ge(S_("ms_ready"), count)
                pool.tensor_tensor(st1[:, slot, 2:3], st1[:, slot, 1:2], mhalf[:], ALU.pow
                                   ).then_inc(S_(name), 1)

            for t in range(CT):
                rsqrt("ss_ready", t + 1, t % 2, 0, "rs_ready", t + 1)
            with pool.Fori(0, NB) as b:
                for t in range(CT):
                    g = b * CT + t
                    cnt = CT + b * 2 * CT + 2 * t + 1
                    pool.wait_ge(S_("ss2_ready"), g + 1)
                    own_instruction(pool)
                    pool.tensor_scalar(st2[:, t % 2, 0:1], st1[:, t % 2, 3:4], 1.0 / D, EPS, ALU.mult,
                                       ALU.add).then_inc(S_("ms2_ready"), 1)
                    pool.wait_ge(S_("ms2_ready"), g + 1)
                    if t >= 2:
                        pool.wait_ge(S_("hn2_ready"), g - 1)
                    else:
                        pool.wait_ge(S_("hn2_ready"), b * CT)
                    pool.tensor_tensor(st2[:, t % 2, 1:2], st2[:, t % 2, 0:1], mhalf[:], ALU.pow
                                       ).then_inc(S_("rs2_ready"), 1)
                    with pool.If(b < NB - 1):
                        rsqrt("ss_ready", (b + 1) * CT + t + 1, t % 2, 0, "rs_ready", (b + 1) * CT + t + 1)

            pool.wait_ge(S_("slots_cleared"), 16)
            pool.wait_ge(S_("spare_cleared"), 16 * (OVMAX + 1) * CAP // 320)
            pool.wait_ge(S_("slots_ready"), 1)
            for t in range(NTILE):
                for j in range(2):
                    pool.indirect_dma_start(
                        slot_d, bass.IndirectOffsetOnAxis(ap=slot_i[:, j, t:t + 1], axis=0), tok[:, t:t + 1], None
                    ).then_inc(S_("slots_written"), 16)
            pool.wait_ge(S_("slots_written"), 16 * 2 * NTILE)
            for i in range(2):
                pool.wait_ge(S_(f"hn2_stored{i}"), 16 * NTILE // 2)

            def gather(k):
                pool.dma_start(idx[:, 0:1], slot_d[bass.ds(k * CAP, P)]).then_inc(S_("idx_loaded"), 16)
                pool.dma_start(idx[0:R1, 1:2], slot_d[bass.ds(k * CAP + P, R1)]).then_inc(S_("idx_loaded"), 16)
                pool.wait_ge(S_("idx_loaded"), 32 * (k + 1))
                pool.wait_ge(S_("xT_done"), 3 * k)
                own_instruction(pool)
                pool.indirect_dma_start(xg[:], None, hn2_d, bass.IndirectOffsetOnAxis(ap=idx[:, 0:1], axis=0)
                                        ).then_inc(S_("x_gathered"), 16)
                pool.indirect_dma_start(xg1[0:R1, :], None, hn2_d,
                                        bass.IndirectOffsetOnAxis(ap=idx[0:R1, 1:2], axis=0)
                                        ).then_inc(S_("x1_gathered"), 16)
                pool.wait_ge(S_("x_gathered"), 16 * (k + 1))
                pool.wait_ge(S_("x1_gathered"), 16 * (k + 1))

            def store(k):
                pool.wait_ge(S_("yr_ready"), 2 * (k + 1))
                pool.dma_start(y_d[bass.ds(k * CAP, P)], yr[:]).then_inc(S_("y_stored"), 16)
                pool.dma_start(y_d[bass.ds(k * CAP + P, R1)], yr1[0:R1, :]).then_inc(S_("y1_stored"), 16)

            pool.wait_ge(S_("routed"), 1)
            n = pool.value_load(n_items[0:1, 0:1], min_val=NE, max_val=NW)
            gather(0)
            with pool.Fori(0, NW) as k:
                with pool.If(k < n):
                    gather(k + 1)
                    store(k)
            store(n)
            pool.wait_ge(S_("y_stored"), 16 * (n + 1))
            pool.wait_ge(S_("y1_stored"), 16 * (n + 1))
            own_instruction(pool)

            for g in range(NTILE):
                if g >= 2:
                    pool.wait_ge(S_("moe_added"), g - 1)
                for j in range(2):
                    pool.indirect_dma_start(yg[j][g % 2], None, y_d,
                                            bass.IndirectOffsetOnAxis(ap=slot_y[:, j, g:g + 1], axis=0)
                                            ).then_inc(S_(f"yg_loaded{g % 2}"), 16)
                if g >= 1:
                    rsqrt("ss3_ready", g, (g - 1) % 2, 0, "rs3_ready", CT * NB + g)
            rsqrt("ss3_ready", NTILE, (NTILE - 1) % 2, 0, "rs3_ready", CT * NB + NTILE)

        @block.vector
        def _(dve):
            def norm_evac(g, t):
                for half in range(2):
                    dve.wait_ge(S_("nT_done"), 2 * g + half + 1)
                    dve.tensor_tensor(hnT[:, 4 * half:4 * half + 4, t * P:(t + 1) * P],
                                      NBANK[half][:].rearrange("p (k t) -> p k t", k=4),
                                      gmix[:, 4 * half:4 * half + 4].unsqueeze(2).broadcast_to([P, 4, P]),
                                      ALU.mult).then_inc(S_("hnT_ready"), 1)

            dve.wait_ge(S_("by_channel_done"), 1)
            dve.tensor_copy(by_channel[:], PROJ[:, 0, 0:NCOL]).then_inc(S_("by_channel_ready"), 1)
            dve.wait_ge(S_("by_channel_ready"), 1)
            dve.wait_ge(S_("masks_ready"), 1)
            for t in range(CT):
                norm_evac(t, t)
            dve.wait_ge(S_("consts_loaded"), 16 * NCONST)
            dve.sem_inc(S_("state_ready"), 1)
            with dve.Fori(0, NB) as b:
                def done(n):
                    dve.wait_ge(S_("proj_done"), b * NU + n + 1)
                    return PROJ[:, n % 2, :]

                E = S_("bank_emptied_dve")
                for h in range(H):
                    ps = done(number[("q", h)])
                    dve.tensor_scalar(qT[:, h, :], ps, bcol[:, 0, h:h + 1], QS, ALU.add, ALU.mult).then_inc(E, 1)
                for s in range(2):
                    for t in range(CT):
                        ps = done(number[("v", (s, t))])
                        dve.tensor_tensor(vx[:, t, 2 * s:2 * s + 2, 0:DH],
                                          ps[:, 0:WC].rearrange("p (h d) -> p h d", h=2),
                                          bvo[:, 0, s * WC:(s + 1) * WC].rearrange("p (h d) -> p h d", h=2),
                                          ALU.add).then_inc(E, 1)
                ps = done(number[("g", 0)])
                dve.tensor_tensor(gt[:], ps[:, 0:CT * 8].rearrange("p (t g) -> p t g", t=CT),
                                  bgt[:].unsqueeze(1).broadcast_to([P, CT, 2 * H]), ALU.add).then_inc(E, 1)

                def o_evac(s):
                    for t in range(CT):
                        ps = done(number[("o", (s, t))])
                        dve.tensor_tensor(og[:, t, s * WC:(s + 1) * WC], ps[:, 0:WC], bvo[:, 1, s * WC:(s + 1) * WC],
                                          ALU.add).then_inc(E, 1)

                o_evac(0)
                step = S_("row_step")
                dve.wait_ge(S_("soft_step"), 3 * b + 3)
                dve.scalar_tensor_tensor(out=rows[7][:, :], in0=RB[0:H, :], scalar=0.0, in1=rows[6][:, :],
                                         op0=ALU.min, op1=ALU.subtract).then_inc(step, 1)
                dve.tensor_copy(mp[:, 0:1], mp[:, CT:CT + 1]).then_inc(step, 1)
                dve.wait_ge(step, 7 * b + 2)
                dve.tensor_tensor_scan(rows[0][:, :], cmask[:], rows[7][:, :], 0.0, ALU.mult, ALU.add
                                       ).then_inc(step, 1)
                dve.tensor_tensor_scan(rows[1][:, :], rows[7][:, :], SC[0:H, :], mp[:, 0:1], ALU.add, ALU.max
                                       ).then_inc(step, 1)
                dve.wait_ge(step, 7 * b + 4)
                dve.tensor_tensor(rows[2][:, :], SC[0:H, :], rows[0][:, :], ALU.subtract
                                  ).then_inc(S_("rows_a_ready"), 1)
                dve.tensor_tensor(rows[3][:, :], rows[0][:, :], rows[1][:, :], ALU.subtract
                                  ).then_inc(S_("rows_m_ready"), 1)
                r3 = rows[3][:, :].rearrange("h (c t) -> h c t", c=CT)
                m3 = rows[1][:, :].rearrange("h (c t) -> h c t", c=CT)
                dve.tensor_copy(mp[:, 1:CT + 1], m3[:, :, P - 1:P].rearrange("h c o -> h (c o)")).then_inc(step, 1)
                dve.wait_ge(S_("rows_a_ready"), b + 1)
                dve.wait_ge(S_("rows_m_ready"), b + 1)
                dve.wait_ge(step, 7 * b + 5)
                r_end = r3[:, :, P - 1:P]
                dve.tensor_tensor(dm[:], r_end.rearrange("h c o -> h (c o)"), mp[:, 0:CT], ALU.add
                                  ).then_inc(S_("dm_ready"), 1)
                dve.tensor_tensor(rows[4][:, :].rearrange("h (c t) -> h c t", c=CT),
                                  rows[2][:, :].rearrange("h (c t) -> h c t", c=CT),
                                  r_end.broadcast_to([H, CT, P]), ALU.add).then_inc(S_("rows_w_ready"), 1)
                dve.wait_ge(S_("decay_ready"), b + 1)
                idb = ident[0:H, 0:H].unsqueeze(1).broadcast_to([H, CT, H])
                dve.tensor_tensor(dg[:, 0], dm[:].unsqueeze(2).broadcast_to([H, CT, H]), idb, ALU.mult
                                  ).then_inc(step, 1)
                dve.tensor_tensor(dg[:, 1], mp[:, 0:CT].unsqueeze(2).broadcast_to([H, CT, H]), idb, ALU.mult
                                  ).then_inc(step, 1)
                dve.wait_ge(step, 7 * b + 7)
                dve.sem_inc(S_("diag_ready"), 1)
                o_evac(1)
                dve.wait_ge(S_("cols_done"), b + 1)
                dve.tensor_copy(cols[:], STA[:, 0, 0:5 * CT * H]).then_inc(S_("cols_ready"), 1)
                dve.wait_ge(S_("cols_ready"), b + 1)
                dve.tensor_copy(uu[:, :, 0:2], uu[:, :, TB:TB + 2]).then_inc(S_("halo_ready"), 1)
                dve.wait_ge(S_("halo_ready"), b + 1)
                EM, DC = 2 * CT * H, 3 * CT * H

                def conv_dve(i):
                    s, i = i // 6, i % 6
                    if i < 2:
                        return
                    m = 2 * s + i % 2
                    if i < 4:
                        ps = done(number[("cx", m)])
                        sm, k_, per = emptied(number[("cc", m)])
                        dve.wait_ge(sm, b * per + k_)
                        dve.scalar_tensor_tensor(out=uu[:, m, 2:TB + 2], in0=ps, scalar=bcol[:, 4, m:m + 1],
                                                 in1=cc[:, m % 2, :], op0=ALU.add, op1=ALU.mult).then_inc(E, 1)
                        return
                    z = S_("conv_step")
                    v = 3 * (b * MT + m)
                    if m % 2 == 0:
                        sm, k_, per = emptied(number[("cx", m + 1)])
                    else:
                        sm, k_, per = emptied(number[("cb", m - 1)])
                    dve.wait_ge(sm, b * per + k_)
                    dve.tensor_scalar(zz[:], uu[:, m, 0:TB], cwc[:, 0, m:m + 1], None, ALU.mult).then_inc(z, 1)
                    for j in (1, 2):
                        dve.wait_ge(z, v + j)
                        dve.scalar_tensor_tensor(out=zz[:], in0=uu[:, m, j:TB + j], scalar=cwc[:, j, m:m + 1],
                                                 in1=zz[:], op0=ALU.mult, op1=ALU.add).then_inc(z, 1)
                    dve.wait_ge(z, v + 3)
                    ps = done(number[("cb", m)])
                    dve.scalar_tensor_tensor(out=yT[:, MT + m, :], in0=ps, scalar=bcol[:, 2, m:m + 1], in1=zz[:],
                                             op0=ALU.add, op1=ALU.mult).then_inc(E, 1)

                for c in range(CT):
                    q = b * CT + c
                    cs = slice(c * P, (c + 1) * P)
                    dve.wait_ge(S_("exp_o_ready"), (b + 1) * 2 * CT)
                    dve.tensor_scalar(og[:, c, :], og[:, c, :], 1.0, None, ALU.add).then_inc(S_("og_step"), 1)
                    dve.wait_ge(S_("scores_done"), q + 1)
                    dve.tensor_tensor(arg[:], RB[:].rearrange("p (h t) -> p h t", h=H),
                                      cneg[:].unsqueeze(1).broadcast_to([P, H, P]), ALU.add
                                      ).then_inc(S_("arg_ready"), 1)
                    dve.wait_ge(S_("og_step"), 2 * q + 1)
                    dve.reciprocal(og[:, c, :], og[:, c, :]).then_inc(S_("og_step"), 1)
                    dve.wait_ge(S_("wint_ready"), q + 1)
                    dve.tensor_tensor(qw[:], qT[:, :, cs], wint[:], ALU.mult).then_inc(S_("qw_ready"), 1)
                    dve.wait_ge(S_("decays_ready"), q + 1)
                    dve.tensor_tensor(arg[:], SC[:].rearrange("p (h t) -> p h t", h=H), arg[:], ALU.mult
                                      ).then_inc(S_("probs_ready"), 1)
                    conv_dve(3 * c)
                    dve.wait_ge(S_("num_done"), q + 1)
                    nv = NUM[:, :, 0:2 * E1].rearrange("p a (h e) -> p a h e", h=2)
                    d = S_("den_step")
                    dv = nv[:, :, :, DH:E1].rearrange("p a h o -> p a (h o)")
                    d0 = den[:, 0, :].rearrange("p (a h) -> p a h", a=2)
                    em = cols[:, EM + c * H:EM + (c + 1) * H].rearrange("p (a h) -> p a h", a=2)
                    dve.scalar_tensor_tensor(out=d0, in0=dv, scalar=-1.0, in1=em, op0=ALU.mult, op1=ALU.max
                                             ).then_inc(d, 1)
                    dve.wait_ge(d, 3 * q + 1)
                    dve.tensor_tensor(d0, dv, d0, ALU.max).then_inc(d, 1)
                    dve.wait_ge(d, 3 * q + 2)
                    dve.reciprocal(den[:, 1, :], den[:, 0, :]).then_inc(d, 1)
                    dve.wait_ge(d, 3 * q + 3)
                    dve.wait_ge(S_("og_step"), 2 * q + 2)
                    if c > 0:
                        dve.wait_ge(S_("ynT_done"), q)
                    for h in range(H):
                        i_ = dve.scalar_tensor_tensor(out=yn[:, h * P:(h + 1) * P],
                                                      in0=nv[:, h // 2, h % 2, 0:DH], scalar=den[:, 1, h:h + 1],
                                                      in1=og[:, c, h * P:(h + 1) * P], op0=ALU.mult, op1=ALU.mult)
                    i_.then_inc(S_("yn_ready"), 1)
                    dve.wait_ge(S_("update_done"), q + 1)
                    dve.wait_ge(S_("state_ready"), q + 1)
                    for h in range(H):
                        o = DC + c * H + h
                        i_ = dve.scalar_tensor_tensor(out=cst[:, h, :], in0=cst[:, h, :], scalar=cols[:, o:o + 1],
                                                      in1=STA[:, h // 2, (h % 2) * E1:(h % 2 + 1) * E1],
                                                      op0=ALU.mult, op1=ALU.add)
                    i_.then_inc(S_("state_ready"), 1)
                    conv_dve(3 * c + 1)
                    conv_dve(3 * c + 2)

                def logits(t):
                    g = b * CT + t
                    dve.wait_ge(S_("logits_done"), g + 1)
                    dve.tensor_tensor(lg[:, bass.ds(g, 1), :].rearrange("p o n -> p (o n)"), STA[:, 0, 0:NR], brt[:],
                                      ALU.add).then_inc(S_("logits_emptied"), 1)

                for t in range(CT):
                    g = b * CT + t
                    dve.wait_ge(S_(f"xres_loaded{t % 2}"), 16 * (2 * b + t // 2 + 1))
                    if t >= 2:
                        dve.wait_ge(S_(f"x2_stored{t % 2}"), 16 * (2 * b + t // 2))
                    else:
                        dve.wait_ge(S_(f"x2_stored{t % 2}"), 32 * b)
                    for half in range(2):
                        ps = done(number[("w", (t, half))])
                        dve.tensor_tensor(x2[t % 2][:, half * 512:(half + 1) * 512], ps,
                                          xres[t % 2][:, half * 512:(half + 1) * 512], ALU.add).then_inc(E, 1)
                    with dve.If(b < NB - 1):
                        norm_evac((b + 1) * CT + t, t)
                    dve.wait_ge(S_("rs2_ready"), g + 1)
                    dve.scalar_tensor_tensor(out=hn2[t % 2][:], in0=x2[t % 2][:], scalar=st2[:, t % 2, 1:2],
                                             in1=gffn[:], op0=ALU.mult, op1=ALU.mult).then_inc(S_("hn2_ready"), 1)
                    if t > 0:
                        logits(t - 1)
                logits(CT - 1)

            rt = S_("route_step")
            count = [0]

            def then(ins):
                count[0] += 1
                ins.then_inc(rt, 1)
                dve.wait_ge(rt, count[0])

            def area(base, at, *shape):
                n = 1
                for s in shape:
                    n *= s
                v = base[:, at:at + n]
                if len(shape) == 2:
                    v = v.rearrange("p (a b) -> p a b", b=shape[1])
                if len(shape) == 3:
                    v = v.rearrange("p (a b c) -> p a b c", b=shape[1], c=shape[2])
                return v

            T = NTILE
            ex = area(routing, 0, T, NG + 1)
            gmax = area(routing, 96, T, 1)
            ohg = area(routing, 112, T, NG)
            pick = area(routing, 176, T, NG)
            pmax = area(routing, 240, T, 1)
            v1 = area(routing, 256, T, 1)
            v2 = area(routing, 272, T, 1)
            v1f, v2f = routing[:, 256:272], routing[:, 272:288]
            se = area(routing, 288, T, EG)
            oh1 = area(routing, 416, T, EG)
            oh2 = area(routing, 544, T, EG)
            pk8 = area(routing, 672, T, EG)
            tot = area(routing, 832, NE, 1)
            totf = routing[:, 832:864]
            nov = routing[:, 864:896]
            ovend = routing[:, 896:928]
            offs = routing[:, 928:960]
            ends = routing[:, 1008:1008 + OVMAX + 1]
            big = area(routing, 1072, T, NE)
            mask = area(routing1, 0, T, NE)
            m1 = area(routing1, 512, T, NE)
            m2 = area(routing1, 1024, T, NE)
            pos = area(routing1, 1536, T, NE)
            dve.wait_ge(S_("logits_emptied"), NTILE)
            dve.wait_ge(S_("route_consts"), 7)
            gl, el = lg[:, :, 0:NG], lg[:, :, NG:NR]
            then(dve.tensor_reduce(gmax, gl, AX.X, ALU.max))
            then(dve.tensor_tensor(ex[:, :, 0:NG], gl, gmax.broadcast_to([P, T, NG]), ALU.subtract))
            o4 = order[:, EG - NG:EG].unsqueeze(1).broadcast_to([P, T, NG])
            o8 = order[:].unsqueeze(1).broadcast_to([P, T, EG])

            def first_of_max(oh, pk, val, mx, od_):
                w = list(oh.shape)
                then(dve.tensor_tensor(pk, val, mx.broadcast_to(w), ALU.is_ge))
                then(dve.tensor_tensor(pk, pk, od_, ALU.mult))
                then(dve.tensor_reduce(pmax, pk, AX.X, ALU.max))
                then(dve.tensor_tensor(oh, pk, pmax.broadcast_to(w), ALU.is_equal))

            first_of_max(ohg, pick, gl, gmax, o4)
            b4 = big.rearrange("p t (e g) -> p t e g", g=NG)
            el4 = el.rearrange("p t (g e) -> p t e g", g=NG)
            for t in range(T):
                then(dve.tensor_tensor(b4[:, t], el4[:, t], ohg[:, t].unsqueeze(1).broadcast_to([P, EG, NG]), ALU.mult))
            then(dve.tensor_reduce(se, b4, AX.X, ALU.add))
            then(dve.tensor_reduce(v1, se, AX.X, ALU.max))
            first_of_max(oh1, pk8, se, v1, o8)
            then(dve.scalar_tensor_tensor(out=se, in0=oh1, scalar=NEG, in1=se, op0=ALU.mult, op1=ALU.add))
            then(dve.tensor_reduce(v2, se, AX.X, ALU.max))
            first_of_max(oh2, pk8, se, v2, o8)
            then(dve.tensor_tensor(ex[:, :, NG:NG + 1], v2, v1, ALU.subtract))
            for mm_, oh in ((m1, oh1), (m2, oh2)):
                for g in range(NG):
                    then(dve.tensor_tensor(mm_[:, :, g * EG:(g + 1) * EG], oh,
                                           ohg[:, :, g:g + 1].broadcast_to([P, T, EG]), ALU.mult))
            then(dve.tensor_tensor(mask, m1, m2, ALU.add))
            dve.sem_inc(S_("mask_ready"), 1)
            dve.sem_inc(S_("route_exp_in"), 1)
            dve.wait_ge(S_("route_exp"), 1)
            then(dve.tensor_reduce(pmax, ex[:, :, 0:NG], AX.X, ALU.add))
            then(dve.tensor_scalar(v1, ex[:, :, NG:NG + 1], 1.0, None, ALU.add))
            then(dve.tensor_tensor(v2, v1, pmax, ALU.mult))
            then(dve.reciprocal(tw[:, 0], v2f))
            then(dve.tensor_tensor(tw[:, 1].unsqueeze(2), ex[:, :, NG:NG + 1], tw[:, 0].unsqueeze(2), ALU.mult))
            dve.wait_ge(S_("ranks_done"), 1)
            then(dve.tensor_copy(pos, SC[:].rearrange("p (t e) -> p t e", t=T)))
            then(dve.memset(totf, 0.0))
            rb = RB[:].rearrange("p (t e) -> p t e", t=T)
            for t in range(T):
                then(dve.tensor_tensor(pos[:, t], pos[:, t], totf, ALU.add))
                then(dve.tensor_tensor(totf, rb[:, t], totf, ALU.add))
            kk = EG * 2
            over = routing[:, 1072:1072 + NE * kk].rearrange("p (e k) -> p e k", k=kk)
            then(dve.tensor_tensor(over, totf.unsqueeze(2).broadcast_to([P, NE, kk]),
                                   ksteps[:].unsqueeze(1).broadcast_to([P, NE, kk]), ALU.is_gt))
            then(dve.tensor_reduce(nov.unsqueeze(2), over, AX.X, ALU.add))
            then(dve.tensor_tensor_scan(ovend, ones[:, 0:NE], nov, 0.0, ALU.mult, ALU.add))
            then(dve.tensor_tensor(offs, ovend, nov, ALU.subtract))
            then(dve.tensor_scalar(offs, offs, float(NE - 1), float(CAP), ALU.add, ALU.mult))
            then(dve.scalar_tensor_tensor(out=offs, in0=eidx[:], scalar=-float(CAP), in1=offs, op0=ALU.mult, op1=ALU.add))
            then(dve.tensor_scalar(big, pos, float(CAP), None, ALU.is_ge))
            then(dve.tensor_tensor(big, big, offs.unsqueeze(1).broadcast_to([P, T, NE]), ALU.mult))
            then(dve.tensor_tensor(pos, pos, big, ALU.add))
            then(dve.tensor_copy(item_e[:, 0:NE], eidx[:]))
            then(dve.tensor_scalar(nov, eidx[:], float(CAP), None, ALU.mult))
            then(dve.tensor_tensor(pos, pos, nov.unsqueeze(1).broadcast_to([P, T, NE]), ALU.add))
            for j, mm_ in enumerate((m1, m2)):
                then(dve.tensor_tensor(mm_, mm_, pos, ALU.mult))
                then(dve.tensor_reduce(v1, mm_, AX.X, ALU.add))
                then(dve.tensor_copy(slot_i[:, j], v1f))
                then(dve.tensor_scalar(v2f, v1f, float(CAP), None, ALU.add))
                then(dve.tensor_copy(slot_y[:, j], v2f))
            then(dve.tensor_scalar(pmax[:, 0], ovend[:, NE - 1:NE], float(NE), None, ALU.add))
            then(dve.tensor_copy(n_items[:], pmax[:, 0]))
            nk = OVMAX + 1
            ov2 = routing[:, 1072:1072 + nk * NE].rearrange("p (k e) -> p k e", e=NE)
            then(dve.tensor_tensor(ov2, ovend.unsqueeze(1).broadcast_to([P, nk, NE]),
                                   item_n[:].unsqueeze(2).broadcast_to([P, nk, NE]), ALU.is_le))
            then(dve.tensor_reduce(ends.unsqueeze(2), ov2, AX.X, ALU.add))
            then(dve.tensor_copy(item_e[:, NE:NE + nk], ends))
            dve.sem_inc(S_("slots_ready"), 1)
            dve.sem_inc(S_("routed"), 1)

            n = dve.value_load(n_items[0:1, 0:1], min_val=NE, max_val=NW)
            DN = [STA[:, 1, :], NUM[:, 0, :], NUM[:, 1, :], STA[:, 0, :]]

            def y_turned(k):
                dve.wait_ge(S_("yrT_done"), k + 1)
                dve.wait_ge(S_("y1_stored"), 16 * k)
                dve.tensor_copy(yr1[0:R1, :], STA[0:R1].rearrange("p a t -> p (a t)")).then_inc(S_("yr_ready"), 1)

            with dve.Fori(0, NW) as k:
                with dve.If(k < n):
                    y_turned(k)
                    for half in range(2):
                        dve.wait_ge(S_("silu_ready"), 2 * k + half + 1)
                        for m in (2 * half, 2 * half + 1):
                            src = [PROJ[:, 0, :], PROJ[:, 1, :], SC[:], RB[:]][m]
                            i_ = dve.tensor_tensor(hT[:, m, :], sgt[:, m, :], src[:, CAP:2 * CAP], ALU.mult)
                        i_.then_inc(S_("hid_ready"), 1)
                    for i in range(2, 4):
                        if i == 2:
                            dve.wait_ge(S_("dn_done"), 3 * k + 3)
                        else:
                            dve.wait_ge(S_("we_used"), (k + 1) * (NWS + FT))
                        dve.tensor_copy(ydT[:, 2 * i:2 * i + 2, :],
                                        DN[i][:, 0:2 * CAP].rearrange("p (k t) -> p k t", k=2)
                                        ).then_inc(S_("yd_ready"), 1)
            y_turned(n)

            def finish(g):
                dve.wait_ge(S_("rs3_ready"), g + 1)
                dve.scalar_tensor_tensor(out=xres[g % 2][:], in0=x2f(g), scalar=st1[:, g % 2, 2:3], in1=gfin[:],
                                         op0=ALU.mult, op1=ALU.mult).then_inc(S_("out_ready"), 1)

            for g in range(NTILE):
                dve.wait_ge(S_(f"yg_loaded{g % 2}"), 32 * (g // 2 + 1))
                dve.wait_ge(S_(f"x2_back{g % 2}"), 16 * (g // 2 + 1))
                dve.scalar_tensor_tensor(out=x2f(g), in0=yg[0][g % 2], scalar=tw[:, 0, g:g + 1], in1=x2[g % 2][:],
                                         op0=ALU.mult, op1=ALU.add).then_inc(S_("add_step"), 1)
                dve.wait_ge(S_("add_step"), g + 1)
                dve.scalar_tensor_tensor(out=x2f(g), in0=yg[1][g % 2], scalar=tw[:, 1, g:g + 1], in1=x2f(g),
                                         op0=ALU.mult, op1=ALU.add).then_inc(S_("moe_added"), 1)
                if g >= 1:
                    finish(g - 1)
            finish(NTILE - 1)


_INS = ["x", "norm_mix", "w_in", "b_in", "conv_w", "w_out", "norm_ffn", "w_group", "b_group",
        "w_expert", "b_expert", "w_gate", "w_up", "w_down", "norm_final"]


def kernel(**inputs):
    import numpy as np
    import concourse.bacc as bacc
    from concourse.bass_utils import run_bass_kernel_spmd

    nc = bacc.Bacc("TRN2", target_bir_lowering=False, num_devices=1)
    arrays, args = {}, []
    for name in _INS:
        a = np.ascontiguousarray(inputs[name])
        arrays[f"in_{name}"] = a
        args.append(nc.dram_tensor(f"in_{name}", a.shape, mybir.dt.from_np(a.dtype), kind="ExternalInput").ap())
    out = nc.dram_tensor("out_rows", inputs["x"].shape, F32, kind="ExternalOutput").ap()
    build(nc, *args, out)
    r = run_bass_kernel_spmd(nc, [arrays], core_ids=[0])
    return r.results[0]["out_rows"]
```
